# Optimizing a Trainium2 kernel written in Bass

```python
import math
import jax, jax.numpy as jnp
from jax import lax
import numpy as np

D_MODEL = 1024
BATCH = 1
SEQ = 1024
DEPTH = 1
DEC_BATCH = 1
DEC_SEQ = 64
PAST_LEN = 2048

CHUNK = 64
NH_A = 4
D_A = 1024
DH_A = D_A // NH_A
D_B = 1024
CONV_W = 31
D_FF = 2816
FFN_CONV_W = 3
EPS = 1e-6
SPLITS = [D_A, 2 * D_A, 3 * D_A, 4 * D_A, 4 * D_A + NH_A, 4 * D_A + 2 * NH_A, 4 * D_A + 2 * NH_A + 2 * D_B]
N_IN = 4 * D_A + 2 * NH_A + 2 * D_B + 2 * D_MODEL

kernel_name = 'mlstm_conformer_hybrid_stream'

def rmsnorm(x, g):
    xf = x.astype(jnp.float32)
    y = xf * lax.rsqrt(jnp.mean(xf * xf, axis=-1, keepdims=True) + EPS)
    return (y * g.astype(jnp.float32)).astype(x.dtype)

def layernorm(x, g, b):
    xf = x.astype(jnp.float32)
    mu = jnp.mean(xf, axis=-1, keepdims=True)
    xc = xf - mu
    y = xc * lax.rsqrt(jnp.mean(xc * xc, axis=-1, keepdims=True) + EPS)
    return (y * g.astype(jnp.float32) + b.astype(jnp.float32)).astype(x.dtype)

def causal_dwconv(x, buf, w, b):
    width = w.shape[0]
    xp = jnp.concatenate([buf.astype(x.dtype), x], axis=1)
    y = lax.conv_general_dilated(xp, w[:, None, :].astype(x.dtype), window_strides=(1,), padding='VALID',
                                 dimension_numbers=('NWC', 'WIO', 'NWC'), feature_group_count=x.shape[-1])
    new_buf = xp[:, xp.shape[1] - (width - 1):]
    return y + b.astype(x.dtype), new_buf

def mlstm_chunk(carry, inp):
    C, n, m = carry
    q, k, v, ig, lf = inp
    L = q.shape[1]
    bcum = jnp.cumsum(lf, axis=1).transpose(0, 2, 1)
    igt = ig.transpose(0, 2, 1)
    logd = bcum[:, :, :, None] - bcum[:, :, None, :] + igt[:, :, None, :]
    causal = jnp.tril(jnp.ones((L, L), dtype=bool))
    logd = jnp.where(causal, logd, -jnp.inf)
    g = bcum + m[:, :, None]
    m_tok = jnp.maximum(g, jnp.max(logd, axis=-1))
    w = jnp.exp(logd - m_tok[..., None])
    inter = jnp.exp(g - m_tok)
    s = jnp.einsum('bjhd,bshd->bhjs', q, k) * w
    inter_blh = inter.transpose(0, 2, 1)
    num = jnp.einsum('bhjs,bshe->bjhe', s, v) + inter_blh[..., None] * jnp.einsum('bjhd,bhde->bjhe', q, C)
    den = jnp.sum(s, axis=-1).transpose(0, 2, 1) + inter_blh * jnp.einsum('bjhd,bhd->bjh', q, n)
    floor = jnp.exp(-m_tok).transpose(0, 2, 1)
    h = num / jnp.maximum(jnp.abs(den), floor)[..., None]
    m_new = m_tok[:, :, -1]
    decay = inter[:, :, -1]
    w_last = w[:, :, -1, :]
    C_new = decay[..., None, None] * C + jnp.einsum('bhs,bshd,bshe->bhde', w_last, k, v)
    n_new = decay[..., None] * n + jnp.einsum('bhs,bshd->bhd', w_last, k)
    return (C_new, n_new, m_new), h

def mlstm(q, k, v, ig, lf, C, n, m):
    B, T, H, D = q.shape
    L = CHUNK if T % CHUNK == 0 else T
    nc = T // L

    def split(a):
        return a.reshape((B, nc, L) + a.shape[2:]).swapaxes(0, 1)

    xs = (split(q), split(k), split(v), split(ig), split(lf))
    (C, n, m), h = lax.scan(mlstm_chunk, (C, n, m), xs)
    h = h.swapaxes(0, 1).reshape(B, T, H, D)
    return h, C, n, m

def layer(x, C, n, m, conv_buf, ffn_buf, p):
    B, T, _ = x.shape
    xn = rmsnorm(x, p['norm_mix_pre'])
    proj = xn @ p['w_in']
    q, k, v, o, ig, fg, u, gates = jnp.split(proj, SPLITS, axis=-1)
    f32 = jnp.float32
    q = q.reshape(B, T, NH_A, DH_A).astype(f32)
    k = k.reshape(B, T, NH_A, DH_A).astype(f32) * (1.0 / math.sqrt(DH_A))
    v = v.reshape(B, T, NH_A, DH_A).astype(f32)
    ig = ig.astype(f32) + p['b_i'].astype(f32)
    lf = jax.nn.log_sigmoid(fg.astype(f32) + p['b_f'].astype(f32))
    h, C, n, m = mlstm(q, k, v, ig, lf, C.astype(f32), n.astype(f32), m.astype(f32))
    h = h * lax.rsqrt(jnp.mean(h * h, axis=-1, keepdims=True) + EPS)
    h = (h.reshape(B, T, D_A) * p['mlstm_norm'].astype(f32)).astype(x.dtype)
    ya = (h * jax.nn.sigmoid(o)) @ p['w_proj_a']
    glu = u[..., :D_B] * jax.nn.sigmoid(u[..., D_B:])
    c, conv_buf = causal_dwconv(glu, conv_buf, p['conv_dw'], p['conv_b'])
    c = jax.nn.silu(layernorm(c, p['conv_ln_g'], p['conv_ln_b']))
    yb = c @ p['w_proj_b'] + p['b_proj_b']
    gt = jax.nn.sigmoid(gates + p['b_merge'])
    mix = (gt[..., :D_MODEL] * ya + gt[..., D_MODEL:] * yb) @ p['w_out']
    x = x + rmsnorm(mix, p['norm_mix_post'])
    hn = rmsnorm(x, p['norm_ffn_pre'])
    up = hn @ p['w_up']
    up, ffn_buf = causal_dwconv(up, ffn_buf, p['ffn_dw'], p['ffn_dw_b'])
    f = (jax.nn.gelu(up[..., :D_FF]) * up[..., D_FF:]) @ p['w_down']
    x = x + rmsnorm(f, p['norm_ffn_post'])
    return x, C, n, m, conv_buf, ffn_buf

def setup_inputs(seed: int = 0) -> dict:
    key = jax.random.key(seed)
    ks = jax.random.split(key, 32)
    nrm = jax.random.normal
    f32 = jnp.float32

    def gain(k, shape):
        return 1.0 + 0.05 * nrm(k, shape, f32)

    return {
        'x_prompt': nrm(ks[0], (BATCH, SEQ, D_MODEL), f32),
        'x_sample': nrm(ks[1], (DEC_BATCH, DEC_SEQ, D_MODEL), f32),
        'state_mlstm_C': 0.05 * nrm(ks[2], (DEPTH, DEC_BATCH, NH_A, DH_A, DH_A), f32),
        'state_mlstm_n': 0.1 * nrm(ks[3], (DEPTH, DEC_BATCH, NH_A, DH_A), f32),
        'state_mlstm_m': jax.random.uniform(ks[4], (DEPTH, DEC_BATCH, NH_A), f32, 0.0, 2.0),
        'cache_conv': 0.5 * nrm(ks[5], (DEPTH, DEC_BATCH, CONV_W - 1, D_B), f32),
        'cache_ffn_conv': nrm(ks[6], (DEPTH, DEC_BATCH, FFN_CONV_W - 1, 2 * D_FF), f32),
        'norm_mix_pre': gain(ks[7], (DEPTH, D_MODEL)),
        'norm_mix_post': gain(ks[8], (DEPTH, D_MODEL)),
        'norm_ffn_pre': gain(ks[9], (DEPTH, D_MODEL)),
        'norm_ffn_post': gain(ks[10], (DEPTH, D_MODEL)),
        'w_in': nrm(ks[11], (DEPTH, D_MODEL, N_IN), f32) * D_MODEL ** -0.5,
        'b_i': 0.1 * nrm(ks[12], (DEPTH, NH_A), f32),
        'b_f': jnp.linspace(3.0, 6.0, NH_A, dtype=f32)[None, :] + 0.1 * nrm(ks[13], (DEPTH, NH_A), f32),
        'mlstm_norm': gain(ks[14], (DEPTH, D_A)),
        'w_proj_a': nrm(ks[15], (DEPTH, D_A, D_MODEL), f32) * D_A ** -0.5,
        'conv_dw': nrm(ks[16], (DEPTH, CONV_W, D_B), f32) * CONV_W ** -0.5,
        'conv_b': 0.02 * nrm(ks[17], (DEPTH, D_B), f32),
        'conv_ln_g': gain(ks[18], (DEPTH, D_B)),
        'conv_ln_b': 0.02 * nrm(ks[19], (DEPTH, D_B), f32),
        'w_proj_b': nrm(ks[20], (DEPTH, D_B, D_MODEL), f32) * D_B ** -0.5,
        'b_proj_b': 0.02 * nrm(ks[21], (DEPTH, D_MODEL), f32),
        'b_merge': 0.1 * nrm(ks[22], (DEPTH, 2 * D_MODEL), f32),
        'w_out': nrm(ks[23], (DEPTH, D_MODEL, D_MODEL), f32) * D_MODEL ** -0.5,
        'w_up': nrm(ks[24], (DEPTH, D_MODEL, 2 * D_FF), f32) * D_MODEL ** -0.5,
        'ffn_dw': nrm(ks[25], (DEPTH, FFN_CONV_W, 2 * D_FF), f32) * FFN_CONV_W ** -0.5,
        'ffn_dw_b': 0.02 * nrm(ks[26], (DEPTH, 2 * D_FF), f32),
        'w_down': nrm(ks[27], (DEPTH, D_FF, D_MODEL), f32) * D_FF ** -0.5,
    }

def reference(x_prompt, x_sample, state_mlstm_C, state_mlstm_n, state_mlstm_m, cache_conv, cache_ffn_conv,
              norm_mix_pre, norm_mix_post, norm_ffn_pre, norm_ffn_post, w_in, b_i, b_f, mlstm_norm, w_proj_a,
              conv_dw, conv_b, conv_ln_g, conv_ln_b, w_proj_b, b_proj_b, b_merge, w_out, w_up, ffn_dw, ffn_dw_b,
              w_down):
    Bp = x_prompt.shape[0]
    yp = x_prompt
    ys = x_sample
    pC, pn, pm, pconv, pffn = [], [], [], [], []
    sC, sn, sm, sconv, sffn = [], [], [], [], []
    for l in range(DEPTH):
        p = {
            'norm_mix_pre': norm_mix_pre[l], 'norm_mix_post': norm_mix_post[l],
            'norm_ffn_pre': norm_ffn_pre[l], 'norm_ffn_post': norm_ffn_post[l],
            'w_in': w_in[l], 'b_i': b_i[l], 'b_f': b_f[l], 'mlstm_norm': mlstm_norm[l],
            'w_proj_a': w_proj_a[l], 'conv_dw': conv_dw[l], 'conv_b': conv_b[l],
            'conv_ln_g': conv_ln_g[l], 'conv_ln_b': conv_ln_b[l], 'w_proj_b': w_proj_b[l],
            'b_proj_b': b_proj_b[l], 'b_merge': b_merge[l], 'w_out': w_out[l], 'w_up': w_up[l],
            'ffn_dw': ffn_dw[l], 'ffn_dw_b': ffn_dw_b[l], 'w_down': w_down[l],
        }
        C0 = jnp.zeros((Bp, NH_A, DH_A, DH_A), jnp.float32)
        n0 = jnp.zeros((Bp, NH_A, DH_A), jnp.float32)
        m0 = jnp.zeros((Bp, NH_A), jnp.float32)
        cb0 = jnp.zeros((Bp, CONV_W - 1, D_B), x_prompt.dtype)
        fb0 = jnp.zeros((Bp, FFN_CONV_W - 1, 2 * D_FF), x_prompt.dtype)
        yp, C1, n1, m1, cb1, fb1 = layer(yp, C0, n0, m0, cb0, fb0, p)
        pC.append(C1); pn.append(n1); pm.append(m1); pconv.append(cb1); pffn.append(fb1)
        ys, C2, n2, m2, cb2, fb2 = layer(ys, state_mlstm_C[l], state_mlstm_n[l], state_mlstm_m[l],
                                         cache_conv[l], cache_ffn_conv[l], p)
        sC.append(C2); sn.append(n2); sm.append(m2); sconv.append(cb2); sffn.append(fb2)
    return (yp, ys,
            jnp.stack(pC), jnp.stack(pn), jnp.stack(pm), jnp.stack(pconv), jnp.stack(pffn),
            jnp.stack(sC), jnp.stack(sn), jnp.stack(sm), jnp.stack(sconv), jnp.stack(sffn))


_drawn_inputs = setup_inputs


def setup_inputs(seed=0):
    import zlib

    import numpy as np

    out = dict(_drawn_inputs(seed))
    spreads = {}
    factors = {'conv_ln_b': 4.615, 'ffn_dw_b': 3.501}
    for name, (base, spread) in spreads.items():
        noise = np.random.default_rng([zlib.crc32(name.encode()), seed]).standard_normal(out[name].shape)
        drawn = base * np.exp(spread * noise) if base else spread * noise
        out[name] = __import__('jax').numpy.asarray(drawn.astype(out[name].dtype))
    for name, factor in factors.items():
        out[name] = (out[name] * factor).astype(out[name].dtype)
    return out
```

```python
from contextlib import ExitStack, contextmanager

import concourse.bass as bass
from concourse import mybir

F32 = mybir.dt.float32
F32R = mybir.dt.float32r
ALU = mybir.AluOpType
ACT = mybir.ActivationFunctionType

P = 128
D = 1024
KB = D // P
SEQ, DEC = 1024, 64
S0 = SEQ + 4
T = S0 + DEC
NC = 3
CH = T // NC
NH, DH = 4, 256
L = 128
NCHUNK = SEQ // L
VW = DH + 2
CW = 31
HALO = CW - 1
GP0, GS0 = HALO, HALO + SEQ + HALO
GW = GS0 + DEC
DFF = 2816
FB = DFF // P
NG = FB // 2
EPS = 1e-6
RW = S0 + L

PV = {n: KB * j for j, n in enumerate(("pre", "post", "fpre", "fpost", "mnorm", "convb", "lng", "lnb",
                                        "bpb", "bga", "bgb"))}
PDW = KB * len(PV)
PFF = PDW + CW * KB
NPAR = PFF + 4 * 2 * FB

N_A, N_A2, N_B, N_C, N_D = 6 * KB, KB, 2 * KB, KB, KB
N_TILES = 1 + N_A + N_A2 + N_B + N_C + N_D + 4 * NG + 2 * NG
CDV = 4 + 2 * CW + 4
CN_SQ = 1 + 3 * KB
GATE_ROWS = 9


class Count:

    made = 0

    def __init__(self, eng, sem, start=0):
        Count.made += 1
        self.name = f"count_{sem.name}_{Count.made}"
        self.eng, self.sem, self.n, self.reg, self.live = eng, sem, start, None, False
        self.early = 0

    def up(self, k):
        self.n += k
        if self.live:
            assert self.early in (0, k), self.name
            if k != self.early:
                self.eng.reg_add(self.reg, self.reg, k)
            self.early = 0
        return self.now()

    def now(self):
        assert not self.early, self.name
        return self.reg if self.live else self.n

    def due(self):
        return self.live or self.n > 0


def settle(count, coming=1):
    if count.live:
        count.eng.reg_add(count.reg, count.reg, coming)
        count.early = coming


@contextmanager
def repeat(eng, times, *counts, ahead=()):
    before = [w.n for w in counts]
    for w in counts:
        if w.reg is None:
            w.reg = eng.alloc_register(w.name)
        w.early = dict(ahead).get(w, 0)
        eng.reg_mov(w.reg, w.n + w.early)
        w.live = True
    with eng.Fori(0, times) as i:
        yield i
    for w, n in zip(counts, before):
        assert w.early == dict(ahead).get(w, 0), w.name
        w.live, w.early = False, 0
        w.n = n + (w.n - n) * times


def build(nc, x, wts, par, gate_par, c_in, conv_halo, ffn_halo, y_out, c_out, m_out,
          conv_tail, ffn_tail):
    scr_h = nc.dram_tensor("scr_heads", (4 * KB, P, T), F32, kind="Internal").ap()
    scr_ga = nc.dram_tensor("scr_gate_a", (KB, P, T), F32, kind="Internal").ap()
    scr_mb = nc.dram_tensor("scr_mix_b", (KB, P, T), F32, kind="Internal").ap()
    scr_z = nc.dram_tensor("scr_z", (KB, P, T), F32, kind="Internal").ap()
    scr_x1 = nc.dram_tensor("scr_x1", (P, KB, T), F32, kind="Internal").ap()
    scr_neg = nc.dram_tensor("scr_neg", (NH, T), F32, kind="Internal").ap()

    base = 16512
    blk = 4 * T
    at_rx, at_rz = base, base + 2 * KB * blk
    at_w = at_rz + 2 * KB * blk
    at_f = at_w + 2 * 4096 + 2 * 8192

    class Room:
        def __init__(self, at):
            self.at = at

        def __call__(self, name, shape, dt=F32):
            n = 4
            for s in shape[1:]:
                n *= s
            t = nc.alloc_sbuf_tensor_at(name, shape, dt, offset=self.at)
            self.at += (n + 31) // 32 * 32
            assert self.at <= 229368, (name, self.at)
            return t

    rx = Room(at_rx)("rx", [P, 2 * KB, T], F32R)
    fx = Room(at_rx)("fx", [P, 2 * KB, T])
    rg = Room(at_rx)("rg", [P, 8, T], F32R)
    rz = Room(at_rz)("rz", [P, 2 * KB, T], F32R)
    fz = Room(at_rz)("fz", [P, 2 * KB, T])
    def block_of(t, k):
        return t[:, :, :].rearrange("p k t -> p (k t)")[:, bass.ds(k * T, T)]

    room = Room(at_w)
    wraw = [room(f"wraw{s}", [P, 1024]) for s in range(2)]
    whi = [room(f"whi{s}", [P, 1024], F32R) for s in range(2)]
    wlo = [room(f"wlo{s}", [P, 1024], F32R) for s in range(2)]
    room = Room(at_f)
    pars = room("pars", [P, NPAR])
    ident = room("ident", [P, P])
    ones = room("ones", [P, P])
    mask = room("mask", [P, L])
    sel = room("sel", [NH, NH, P])
    gt = room("gt", [P, (NCHUNK + 1) * 16])
    decs = room("decs", [P, NH, NCHUNK + 1])
    eps = room("eps", [P, 1])
    nbgb = room("nbgb", [P, KB])
    gpar = room("gpar", [NH, 4])
    mouts = room("mouts", [NH, 2])
    drow = room("drow", [NH, 16])
    zpad = room("zpad", [P, KB, S0 - SEQ])
    fhalo = room("fhalo", [P, 4 * FB])
    at_s = room.at

    room = Room(at_s)
    sta = room("sta", [P, T])
    stb = room("stb", [P, T])
    spl = [room(f"spl{s}", [P, T]) for s in range(2)]
    glub = room("glub", [P, GW])
    cacc = room("cacc", [P, T])
    csum = room("csum", [P, T])
    g4 = room("g4", [P, RW])
    chalo = room("chalo", [P, KB * HALO])
    row3 = room("row3", [P, T])
    ctail = Room(room.at - (4 * T + 31) // 32 * 32)("ctail", [P, KB * 2 * HALO])
    wcur = Room(at_rz)("wcur", [P, 32])
    csq = Room(at_rz + 4096)("csq", [P, T])
    sqt = Room(at_rz + 4096 + 4608)("sqt", [P, T])

    room = Room(at_s)
    ntmp = room("ntmp", [P, KB, CH])
    rst = [room(f"rst{c}", [P, CH]) for c in range(NC)]
    osq = [room(f"osq{s}", [P, CH]) for s in range(2)]
    oss = room("oss", [P, T])

    room = Room(at_s)
    qkv = room("qkv", [P, 2, 3, L])
    ob = room("ob", [P, 2, L])
    qkh = [room(f"qkh{s}", [P, 2, 2, L], F32R) for s in range(2)]
    qkl = [room(f"qkl{s}", [P, 2, 2, L], F32R) for s in range(2)]
    wt = room("wt", [P, L])
    ah = room("ah", [P, L], F32R)
    al = room("al", [P, L], F32R)
    kh = room("kh", [P, DH], F32R)
    kl = room("kl", [P, DH], F32R)
    vh = room("vh", [P, VW], F32R)
    vl = room("vl", [P, VW], F32R)
    c32 = room("c32", [P, NH, 2, VW])
    ch = room("ch", [P, 2, VW], F32R)
    cl = room("cl", [P, 2, VW], F32R)
    hn = room("hn", [P, VW])
    zt = room("zt", [P, DH])
    zs = room("zs", [P, 2, L])
    negc = room("negc", [NH, L])
    gtc = room("gtc", [P, 16])
    dcc = room("dcc", [P, NH])
    sm = room("sm", [P, 8])
    sigb = room("sigb", [P, T])
    ybs = room("ybs", [P, CH])

    room = Room(at_s)
    zl = [room(f"zl{s}", [P, T]) for s in range(2)]
    gal = [room(f"gal{s}", [P, T]) for s in range(2)]
    mbl = [room(f"mbl{s}", [P, T]) for s in range(2)]
    yas = [room(f"yas{s}", [P, T]) for s in range(2)]

    room = Room(at_s)
    ub = [room(f"ub{s}", [P, T + 2]) for s in range(2)]
    cv = [room(f"cv{s}", [P, T]) for s in range(2)]
    fcur = room("fcur", [P, 4])
    ftail = room("ftail", [P, 8 * FB])

    with ExitStack() as ctx:
        ps = ctx.enter_context(nc.psum_tensor("ps", [P, 8 * 512], F32))

        def bank(b, a=0, n=512):
            return ps[:, b * 512 + a:b * 512 + a + n]

        def sem(name):
            return ctx.enter_context(nc.semaphore(name))

        raw_in = [sem(f"raw_in{s}") for s in range(2)]
        split_hi = sem("split_hi")
        split_done = sem("split_done")
        tbank_full = sem("tbank_full")
        tbank_free = sem("tbank_free")
        dbank_full = sem("dbank_full")
        dbank_free = sem("dbank_free")
        const_in = sem("const_in")
        const_set = sem("const_set")
        x_in = [sem(f"x_in{c}") for c in range(NC)]
        sq_set = sem("sq_set")
        ms_full = sem("ms_full")
        lnr = sem("lnr")
        r_set = sem("r_set")
        xs_set = sem("xs_set")
        nhi = sem("nhi")
        nlo = sem("nlo")
        gate_row = sem("gate_row")
        gate_dve = sem("gate_dve")
        neg_out = sem("neg_out")
        g4_t = sem("g4_t")
        gt_set = sem("gt_set")
        stab_free = sem("stab_free")
        spl_out = [sem(f"spl_out{s}") for s in range(2)]
        cdv0 = sem("cdv0")
        cdv = sem("cdv")
        tail_out = sem("tail_out")
        mu_full = sem("mu_full")
        mu_set = sem("mu_set")
        cn_set = sem("cn_set")
        csig = sem("csig")
        chi = sem("chi")
        clo_b = sem("clo_b")
        qkv_in = sem("qkv_in")
        o_in = sem("o_in")
        neg_in = sem("neg_in")
        c_ld = sem("c_ld")
        c_st = sem("c_st")
        qkhi = sem("qkhi")
        qklo = sem("qklo")
        kv_full = sem("kv_full")
        s_full = sem("s_full")
        vkhi = sem("vkhi")
        wexp = sem("wexp")
        cahi = sem("cahi")
        wneg = sem("wneg")
        kvlo = sem("kvlo")
        a32 = sem("a32")
        alo = sem("alo")
        n_full = sem("n_full")
        t1_set = sem("t1_set")
        hn_set = sem("hn_set")
        dsm = sem("dsm")
        ssq = sem("ssq")
        vlog = sem("vlog")
        rs_set = sem("rs_set")
        cupd = sem("cupd")
        zt_set = sem("zt_set")
        z_full = sem("z_full")
        zs_set = sem("zs_set")
        z_out = sem("z_out")
        sig_step = sem("sig_step")
        mixb = sem("mixb")
        mixb_out = sem("mixb_out")
        zl_in = [sem(f"zl_in{s}") for s in range(2)]
        zhi = sem("zhi")
        zlo = sem("zlo")
        ga_in = [sem(f"ga_in{s}") for s in range(2)]
        mb_in = [sem(f"mb_in{s}") for s in range(2)]
        mix_step = sem("mix_step")
        mixhi = sem("mixhi")
        mixlo = sem("mixlo")
        osq_set = sem("osq_set")
        oss_set = sem("oss_set")
        gtc_set = sem("gtc_set")
        orr = sem("orr")
        x1_set = sem("x1_set")
        x1g = sem("x1g")
        x1_out = sem("x1_out")
        fdv = sem("fdv")
        conv_step = sem("conv_step")
        conv_set = sem("conv_set")
        gelu_set = sem("gelu_set")
        g32 = sem("g32")
        ghi = sem("ghi")
        glo = sem("glo")
        y_set = sem("y_set")
        y_sto = sem("y_sto")

        block = ctx.enter_context(nc.Block())

        @block.sync
        def _(sp):
            split = Count(sp, split_done, start=-2)
            evac = Count(sp, tbank_free)
            state = {"t": 0}

            def fetch(index):
                slot = state["t"] % 2
                state["t"] += 1
                split.up(1)
                if split.due():
                    sp.wait_ge(split_done, split.now())
                sp.dma_start(wraw[slot][:, :], wts[index]).then_inc(raw_in[slot], 16)

            def fetch_static(n):
                for _ in range(n):
                    fetch(state["t"])

            for c in range(NC):
                sp.dma_start(fz[:, 0:KB, c * CH:(c + 1) * CH], x[:, :, c * CH:(c + 1) * CH]).then_inc(x_in[c], 16)
                if c == 0:
                    sp.dma_start(pars[:, :], par).then_inc(const_in, 16)
                    sp.dma_start(gpar[:, :], gate_par).then_inc(const_in, 16)
            fetch_static(2)
            sp.dma_start(chalo[:, :], conv_halo).then_inc(const_in, 16)
            sp.dma_start(fhalo[:, :], ffn_halo).then_inc(const_in, 16)
            fetch_static(1)
            fetch_static(1)
            evac.up(3)
            for sem_ in (*spl_out, z_out, mixb_out):
                sp.sem_inc(sem_, 16)
            gd = Count(sp, gate_dve)
            sp.wait_ge(gate_dve, gd.up(10))
            sp.dma_start(scr_neg, csum[0:NH, 0:T]).then_inc(neg_out, 16)
            first = state["t"]
            with repeat(sp, KB, split, evac) as i:
                for pos in range(6):
                    fetch(i * 6 + (first + pos))
                    if pos < 2:
                        evac.up(3)
                    else:
                        sp.wait_ge(tbank_free, evac.up(3))
                        sp.dma_start(scr_h[i * 4 + (pos - 2)], spl[pos % 2][:, :]).then_inc(spl_out[pos % 2], 16)
            state["t"] = first + N_A
            cd = Count(sp, cdv)
            sp.wait_ge(cdv, cd.up(KB * CDV))
            cst = Count(sp, const_set)
            sp.wait_ge(const_set, cst.up(9))
            sp.dma_start(scr_z[:, :, SEQ:S0].rearrange("k p n -> p k n"), zpad[:, :, :]).then_inc(tail_out, 16)
            for g in range(2):
                sp.dma_start(conv_tail[g], ctail[:, :].rearrange("p (k n) -> p k n", k=KB)[:, :, g * HALO:(g + 1) * HALO]).then_inc(tail_out, 16)
            sp.wait_ge(gate_dve, gd.up(1))
            sp.dma_start(m_out, mouts[:, :]).then_inc(tail_out, 16)
            for half in range(2):
                first = state["t"]
                with repeat(sp, KB // 4, split, evac) as i:
                    for pos in range(2):
                        fetch(i * 2 + (first + pos))
                        sp.wait_ge(tbank_free, evac.up(3))
                        sp.dma_start(scr_ga[i * 2 + (pos + half * KB // 2)], spl[pos % 2][:, :])\
                            .then_inc(spl_out[pos % 2], 16)
                state["t"] = first + KB // 2
            qk = Count(sp, qklo)
            kv = Count(sp, kv_full)
            ss = Count(sp, s_full)
            zd = Count(sp, zs_set)
            mbw = Count(sp, mixb)
            cup = Count(sp, cupd)
            kvs = Count(sp, vkhi)
            so = [Count(sp, spl_out[s]) for s in range(2)]
            for s in range(2):
                sp.wait_ge(spl_out[s], so[s].up(16 * (1 + 2 * KB + KB // 2)))
            cl_w = Count(sp, clo_b)
            sp.wait_ge(clo_b, cl_w.up(KB))
            no = Count(sp, neg_out)
            to = Count(sp, tail_out)
            no.up(16), to.up(64)
            sp.wait_ge(neg_out, no.now())
            sp.wait_ge(tail_out, to.now())

            def load_qkv(h, cols, n):
                for b in range(2):
                    sp.dma_start(qkv[:, b, :, 0:n],
                                 scr_h[8 * h + 4 * b:8 * h + 4 * b + 3, :, cols].rearrange("t p n -> p t n"))\
                        .then_inc(qkv_in, 16)

            def load_o(h, cols, n):
                for b in range(2):
                    sp.dma_start(ob[:, b, 0:n], scr_h[8 * h + 4 * b + 3, :, cols]).then_inc(o_in, 16)

            def store_z(h, cols, n):
                sp.wait_ge(zs_set, zd.up(2))
                sp.dma_start(scr_z[2 * h:2 * h + 2, :, cols].rearrange("b p n -> p b n"), zs[:, :, 0:n])\
                    .then_inc(z_out, 16)

            def mlstm(cols, n, get, later):
                sp.dma_start(negc[:, 0:n], scr_neg[:, cols]).then_inc(neg_in, 16)
                load_qkv(0, cols, n)
                load_o(0, cols, n)
                get()
                ss.up(1), qk.up(1)
                sp.wait_ge(s_full, ss.now())
                sp.wait_ge(qklo, qk.now())
                load_qkv(1, cols, n)
                ss.up(1), qk.up(1)
                sp.wait_ge(s_full, ss.now())
                sp.wait_ge(qklo, qk.now())
                load_qkv(2, cols, n)
                store_z(0, cols, n)
                load_o(1, cols, n)
                get()
                ss.up(1), qk.up(1)
                sp.wait_ge(s_full, ss.now())
                sp.wait_ge(qklo, qk.now())
                load_qkv(3, cols, n)
                store_z(1, cols, n)
                load_o(2, cols, n)
                store_z(2, cols, n)
                load_o(3, cols, n)
                store_z(3, cols, n)
                later()

            first = state["t"]
            with repeat(sp, NCHUNK, split, ss, qk, zd, mbw) as i:
                pos = iter(range(2))

                def get():
                    fetch(i * 2 + (first + next(pos)))

                def later():
                    ss.up(1), qk.up(1), mbw.up(3)
                    sp.wait_ge(s_full, ss.now())
                    sp.wait_ge(qklo, qk.now())
                    sp.wait_ge(mixb, mbw.now())
                    sp.dma_start(scr_mb[i], sigb[:, :]).then_inc(mixb_out, 16)

                mlstm(bass.ds(i * L, L), L, get, later)
            state["t"] = first + N_B
            sp.wait_ge(cupd, cup.up(NH * 2 * NCHUNK))
            sp.dma_start(c_out[0], c32[:, :, :, :]).then_inc(c_st, 16)
            cs = Count(sp, c_st)
            sp.wait_ge(c_st, cs.up(16))
            sp.dma_start(c32[:, :, :, :], c_in).then_inc(c_ld, 16)
            mlstm(slice(S0, T), DEC, lambda: None, lambda: None)
            ss.up(1), qk.up(1), cup.up(NH * 2)
            sp.wait_ge(s_full, ss.now())
            sp.wait_ge(qklo, qk.now())
            sp.wait_ge(cupd, cup.now())
            sp.dma_start(c_out[1], c32[:, :, :, :]).then_inc(c_st, 16)
            zo = Count(sp, z_out)
            mo = Count(sp, mixb_out)
            cs.up(16), zo.up(16 * (1 + NH * (NCHUNK + 1))), mo.up(16 * (NCHUNK + 1))
            sp.wait_ge(c_st, cs.now())
            sp.wait_ge(z_out, zo.now())
            sp.wait_ge(mixb_out, mo.now())
            zlw = Count(sp, zlo, start=-2)
            for k in range(KB):
                zlw.up(1)
                if zlw.due():
                    sp.wait_ge(zlo, zlw.now())
                sp.dma_start(zl[k % 2][:, :], scr_z[k]).then_inc(zl_in[k % 2], 16)
            mx = Count(sp, mixlo, start=-2)
            for s in range(2):
                sp.dma_start(gal[s][:, :], scr_ga[s]).then_inc(ga_in[s], 16)
                sp.dma_start(mbl[s][:, :], scr_mb[s]).then_inc(mb_in[s], 16)
            mx.up(2)
            first = state["t"]
            with repeat(sp, KB // 2 - 1, split, mx) as i:
                for pos in range(2):
                    fetch(i * 2 + (first + pos))
                    mx.up(1)
                    if mx.due():
                        sp.wait_ge(mixlo, mx.now())
                    sp.dma_start(gal[pos][:, :], scr_ga[i * 2 + (2 + pos)]).then_inc(ga_in[pos], 16)
                    sp.dma_start(mbl[pos][:, :], scr_mb[i * 2 + (2 + pos)]).then_inc(mb_in[pos], 16)
            state["t"] = first + KB - 2
            fetch_static(2)
            fetch_static(1)
            mlw = Count(sp, tbank_full, start=3 * (1 + N_A + N_A2 + N_B))
            sp.wait_ge(tbank_full, mlw.up(3 * N_C))
            for c in range(NC):
                sp.dma_start(fx[:, KB:2 * KB, c * CH:(c + 1) * CH], x[:, :, c * CH:(c + 1) * CH]).then_inc(x_in[c], 16)
            first = state["t"]
            with repeat(sp, 3, split) as i:
                for pos in range(2):
                    fetch(i * 2 + (first + pos))
            state["t"] = first + 6
            fetch_static(1)
            x1w = Count(sp, x1_set)
            for c in range(NC):
                sp.wait_ge(x1_set, x1w.up(1))
                sp.dma_start(scr_x1[:, :, c * CH:(c + 1) * CH], fx[:, KB:2 * KB, c * CH:(c + 1) * CH])\
                    .then_inc(x1_out, 16)
            rest = N_TILES - state["t"]
            first = state["t"]
            with repeat(sp, rest // 2, split) as i:
                for pos in range(2):
                    fetch(i * 2 + (first + pos))
            state["t"] = first + rest // 2 * 2
            fetch_static(rest % 2)
            dfw = Count(sp, dbank_full)
            x1o = Count(sp, x1_out)
            dfw.up(24 * NG), x1o.up(16 * NC)
            sp.wait_ge(dbank_full, dfw.now())
            sp.wait_ge(x1_out, x1o.now())
            for c in range(NC):
                sp.dma_start(fx[:, 0:KB, c * CH:(c + 1) * CH], scr_x1[:, :, c * CH:(c + 1) * CH]).then_inc(x_in[c], 16)
            fdw = Count(sp, fdv)
            sp.wait_ge(fdv, fdw.up(2 + 3 * 2 * FB))
            sp.dma_start(ffn_tail, ftail[:, :]).then_inc(y_sto, 16)
            yw = Count(sp, y_set)
            for c in range(NC):
                sp.wait_ge(y_set, yw.up(1))
                sp.dma_start(y_out[:, :, c * CH:(c + 1) * CH], fx[:, 0:KB, c * CH:(c + 1) * CH]).then_inc(y_sto, 16)
            sp.wait_ge(y_sto, 16 * (NC + 1))
            sp.wait_ge(c_st, 32)
            sp.wait_ge(tail_out, 64)

        @block.gpsimd
        def _(pool):
            step = Count(pool, const_set)
            pool.memset(ones[:, :], 1.0).then_inc(const_set, 1)
            pool.memset(ident[:, :], 0.0).then_inc(const_set, 1)
            pool.memset(mask[:, :], 0.0).then_inc(const_set, 1)
            pool.memset(sel[:, :, :], 0.0).then_inc(const_set, 1)
            pool.memset(eps[:, :], EPS).then_inc(const_set, 1)
            pool.memset(zpad[:, :, :], 0.0).then_inc(const_set, 1)
            pool.wait_ge(const_set, step.up(6))
            pool.affine_select(out=ident[:, :], in_=ident[:, :], compare_op=ALU.not_equal, fill=1.0,
                               base=0, pattern=[[-1, P]], channel_multiplier=1).then_inc(const_set, 1)
            pool.affine_select(out=mask[:, :], in_=mask[:, :], compare_op=ALU.is_ge, fill=-1e30,
                               base=0, pattern=[[1, L]], channel_multiplier=-1).then_inc(const_set, 1)
            pool.affine_select(out=sel[:, :, :], in_=sel[:, :, :], compare_op=ALU.not_equal, fill=1.0,
                               base=0, pattern=[[-1, NH], [0, P]], channel_multiplier=1).then_inc(const_set, 1)
            raw = [Count(pool, raw_in[s]) for s in range(2)]
            hi_w = Count(pool, split_hi)
            tb = Count(pool, tbank_full, start=-6)
            db = Count(pool, dbank_full)
            n = [0]

            def split(down):
                s = n[0] % 2
                n[0] += 1
                if down:
                    raw[s].up(16), db.up(12)
                    pool.wait_ge(raw_in[s], raw[s].now())
                    pool.wait_ge(dbank_full, db.now())
                else:
                    raw[s].up(16), tb.up(3)
                    pool.wait_ge(raw_in[s], raw[s].now())
                    if tb.due():
                        pool.wait_ge(tbank_full, tb.now())
                settle(raw[s], 16)
                pool.tensor_copy(whi[s][:, :], wraw[s][:, :]).then_inc(split_hi, 1)
                pool.wait_ge(split_hi, hi_w.up(1))
                pool.tensor_tensor(wlo[s][:, :], wraw[s][:, :], whi[s][:, :].bitcast(F32), ALU.subtract)\
                    .then_inc(split_done, 1)

            for _ in range(3):
                split(False)
            upto = N_TILES - 6 * (NG - 1)
            with repeat(pool, (upto - 3) // 2, *raw, hi_w, tb, ahead=[(r, 16) for r in raw]) as i:
                for _ in range(2):
                    split(False)
            n[0] = upto
            with repeat(pool, NG - 1, *raw, hi_w, tb, db, ahead=[(r, 16) for r in raw]) as i:
                for down in (False, False, True, False, False, True):
                    split(down)

        @block.tensor
        def _(pe):
            ready = Count(pe, split_done)
            free = Count(pe, tbank_free, start=-2)
            dfree = Count(pe, dbank_free, start=-4)
            n = {"slot": 0, "t": 0, "d": 0}
            cst = Count(pe, const_set)
            pe.wait_ge(const_set, cst.up(9))

            def group(s, src, c):
                free.up(1)
                if free.due():
                    pe.wait_ge(tbank_free, free.now())
                b = n["t"] % 2
                n["t"] += 1
                cols = slice(c * CH, (c + 1) * CH)
                for k in range(KB):
                    w = slice(k * P, (k + 1) * P)
                    pe.matmul(bank(b, 0, CH), whi[s][:, w], src[:, k, cols], start=(k == 0), stop=False)
                    pe.matmul(bank(b, 0, CH), whi[s][:, w], src[:, KB + k, cols], start=False, stop=False)
                    mm = pe.matmul(bank(b, 0, CH), wlo[s][:, w], src[:, k, cols], start=False, stop=(k == KB - 1))
                mm.then_inc(tbank_full, 1)

            def groups(src):
                s = n["slot"] % 2
                n["slot"] += 1
                pe.wait_ge(split_done, ready.up(1))
                for c in range(NC):
                    group(s, src, c)
                    yield

            def tile(src):
                for _ in groups(src):
                    pass

            def sums(c, src, blocks, sem_):
                for k in range(blocks):
                    mm = pe.matmul(bank(2 + c, 0, CH), ones[:, :], src(k), start=(k == 0), stop=(k == blocks - 1))
                mm.then_inc(sem_, 1)

            sqw = Count(pe, sq_set)
            for c in range(NC):
                pe.wait_ge(sq_set, sqw.up(1))
                sums(c, lambda k: ntmp[:, k, :], KB, ms_full)
            nl = Count(pe, nlo)
            pe.wait_ge(split_done, ready.up(1))
            for c in range(NC):
                pe.wait_ge(nlo, nl.up(1))
                group(0, rx, c)
            n["slot"] = 1
            with repeat(pe, KB, ready, free) as i:
                for _ in range(6):
                    tile(rx)
            gr = Count(pe, gate_row)
            gd = Count(pe, gate_dve)
            gr.up(GATE_ROWS), gd.up(12)
            pe.wait_ge(gate_row, gr.now())
            pe.wait_ge(gate_dve, gd.now())
            for c in range(NCHUNK + 1):
                at = c * L if c < NCHUNK else S0
                mm = pe.transpose(bank(5, 0, 1536)[:, c * P:(c + 1) * P], g4[:, at:at + L], ident[:, :])
            mm = None
            for h in range(NH):
                mm = pe.matmul(bank(7, 256 + 16 * h, NCHUNK + 1), sel[:, h, :], drow[:, 0:NCHUNK + 1],
                               start=True, stop=True)
            mm.then_inc(g4_t, 1)
            cd = Count(pe, cdv)
            pe.wait_ge(cdv, cd.up(KB * CDV))
            for c in range(NC):
                sums(c, lambda k: csum[:, c * CH:(c + 1) * CH], 1, mu_full)
            with repeat(pe, KB // 4, ready, free) as i:
                for _ in range(2):
                    tile(rx)
            cn = Count(pe, cn_set)
            pe.wait_ge(cn_set, cn.up(CN_SQ))
            for c in range(NC):
                sums(c, lambda k: csq[:, c * CH:(c + 1) * CH], 1, mu_full)
            with repeat(pe, KB // 4, ready, free) as i:
                for _ in range(2):
                    tile(rx)

            qk = Count(pe, qklo)
            al_w = Count(pe, alo)
            ztw = Count(pe, zt_set)
            zs_w = Count(pe, zs_set)

            def scores(h):
                pe.wait_ge(qklo, qk.up(1))
                s = h % 2
                for j, ty in enumerate((1, 2)):
                    for b in range(2):
                        mm = pe.transpose(bank(2, (2 * j + b) * P, P), qkv[:, b, ty, :], ident[:, :])
                mm.then_inc(kv_full, 1)
                pe.matmul(bank(3, 0, L), sel[:, h, :], negc[:, :], start=True, stop=True)
                for b in range(2):
                    k_hi, k_lo = qkh[s][:, b, 1, :], qkl[s][:, b, 1, :]
                    q_hi, q_lo = qkh[s][:, b, 0, :], qkl[s][:, b, 0, :]
                    pe.matmul(bank(3, L, L), k_hi, q_hi, start=(b == 0), stop=False)
                    pe.matmul(bank(3, L, L), k_hi, q_lo, start=False, stop=False)
                    mm = pe.matmul(bank(3, L, L), k_lo, q_hi, start=False, stop=(b == 1))
                mm.then_inc(s_full, 1)

            def values(h):
                pe.wait_ge(alo, al_w.up(1))
                s = h % 2
                for b in range(2):
                    q_hi, q_lo = qkh[s][:, b, 0, :], qkl[s][:, b, 0, :]
                    pe.matmul(bank(5, 0, VW), q_hi, ch[:, b, :], start=(b == 0), stop=False)
                    pe.matmul(bank(5, 0, VW), q_hi, cl[:, b, :], start=False, stop=False)
                    pe.matmul(bank(5, 0, VW), q_lo, ch[:, b, :], start=False, stop=(b == 1))
                pe.matmul(bank(4, 0, VW), ah[:, :], vh[:, :], start=True, stop=False)
                pe.matmul(bank(4, 0, VW), ah[:, :], vl[:, :], start=False, stop=False)
                pe.matmul(bank(4, 0, VW), al[:, :], vh[:, :], start=False, stop=True)
                for b in range(2):
                    kb = slice(b * P, (b + 1) * P)
                    pe.matmul(bank(6 + b, 0, VW), kh[:, kb], vh[:, :], start=True, stop=False)
                    pe.matmul(bank(6 + b, 0, VW), kh[:, kb], vl[:, :], start=False, stop=False)
                    mm = pe.matmul(bank(6 + b, 0, VW), kl[:, kb], vh[:, :], start=False, stop=True)
                mm.then_inc(n_full, 1)

            def rows(h):
                pe.wait_ge(zt_set, ztw.up(1))
                for b in range(2):
                    mm = pe.transpose(bank(3, 256 + b * L, L), zt[:, b * P:(b + 1) * P], ident[:, :])
                mm.then_inc(z_full, 1)

            def mlstm(go):
                go()
                scores(0)
                go()
                values(0), scores(1)
                go()
                values(1), rows(0)
                pe.wait_ge(zs_set, zs_w.up(2))
                scores(2)
                go()
                values(2), rows(1)
                pe.wait_ge(zs_set, zs_w.up(2))
                scores(3)
                go()
                values(3), rows(2)
                go()
                rows(3)
                zs_w.up(4)

            cbw = Count(pe, clo_b)
            pe.wait_ge(clo_b, cbw.up(KB))
            with repeat(pe, NCHUNK, ready, free, qk, al_w, ztw, zs_w) as i:
                def steps():
                    yield from groups(rx)
                    yield from groups(rz)
                it = steps()
                mlstm(lambda: next(it))
                assert next(it, "end") == "end"
            mlstm(lambda: None)

            zw = Count(pe, zlo)
            pe.wait_ge(zlo, zw.up(KB))
            with repeat(pe, KB // 2, ready, free) as i:
                for _ in range(2):
                    tile(rx)
            mw = Count(pe, mixlo)
            pe.wait_ge(mixlo, mw.up(KB))
            with repeat(pe, KB // 2, ready, free) as i:
                for _ in range(2):
                    tile(rz)
            ow = Count(pe, oss_set)
            pe.wait_ge(oss_set, ow.up(1 + 3 * KB))
            for c in range(NC):
                sums(c, lambda k: oss[:, c * CH:(c + 1) * CH], 1, ms_full)
            for c in range(NC):
                pe.wait_ge(sq_set, sqw.up(1))
                sums(c, lambda k: ntmp[:, k, :], KB, ms_full)

            gl = Count(pe, glo)

            def down(par):
                s = n["slot"] % 2
                n["slot"] += 1
                pe.wait_ge(split_done, ready.up(1))
                for m in range(4):
                    for c in range(NC):
                        dfree.up(1)
                        if dfree.due():
                            pe.wait_ge(dbank_free, dfree.now())
                        b = 2 + n["d"] % 4
                        n["d"] += 1
                        cols = slice(c * CH, (c + 1) * CH)
                        for k in range(2):
                            w = slice((k * 4 + m) * P, (k * 4 + m + 1) * P)
                            j = 2 * par + k
                            pe.matmul(bank(b, 0, CH), whi[s][:, w], rg[:, j, cols], start=(k == 0), stop=False)
                            pe.matmul(bank(b, 0, CH), whi[s][:, w], rg[:, 4 + j, cols], start=False, stop=False)
                            mm = pe.matmul(bank(b, 0, CH), wlo[s][:, w], rg[:, j, cols], start=False, stop=(k == 1))
                        mm.then_inc(dbank_full, 1)

            s = n["slot"] % 2
            n["slot"] += 1
            pe.wait_ge(split_done, ready.up(1))
            for c in range(NC):
                pe.wait_ge(nlo, nl.up(1))
                group(s, rz, c)
            for _ in range(5):
                tile(rz)

            def turn(par, last=False):
                pe.wait_ge(glo, gl.up(2))
                down(par)
                tile(rz), tile(rz)
                down(par)
                if not last:
                    tile(rz), tile(rz)

            turn(0)
            with repeat(pe, (NG - 3) // 2, ready, free, dfree, gl) as i:
                turn(1)
                turn(0)
            turn(1, last=True)
            pe.wait_ge(glo, gl.up(2))
            down(0)
            down(0)
            for c in range(NC):
                pe.wait_ge(sq_set, sqw.up(1))
                sums(c, lambda k: ntmp[:, k, :], KB, ms_full)

        @block.scalar
        def _(act):
            full = Count(act, tbank_full)
            n = {"t": 0}

            def evac(dst, func=ACT.Identity, bias=0.0, scale=1.0, rows_=slice(0, P)):
                b = n["t"] % 2
                return act.activation(dst, bank(b, 0, CH)[rows_, :], func, bias=bias, scale=scale)

            def evac_tile(dst, func=ACT.Identity, bias=0.0, scale=1.0, off=0):
                for c in range(NC):
                    act.wait_ge(tbank_full, full.up(1))
                    if not isinstance(bias, float):
                        settle(full)
                    evac(dst[:, off + c * CH:off + (c + 1) * CH], func, bias, scale).then_inc(tbank_free, 1)
                    n["t"] += 1

            ln_w = Count(act, lnr)
            ms = Count(act, ms_full)

            def root(c, width=D):
                act.wait_ge(ms_full, ms.up(1))
                act.activation(rst[c][:, :], bank(2 + c, 0, CH), ACT.Ln, bias=eps[:, 0:1], scale=1.0 / width)\
                    .then_inc(lnr, 1)
                act.wait_ge(lnr, ln_w.up(1))
                act.activation(rst[c][:, :], rst[c][:, :], ACT.Exp, scale=-0.5).then_inc(r_set, 1)

            cst = Count(act, const_set)
            cin = Count(act, const_in)
            act.wait_ge(const_set, cst.up(9))
            xs = Count(act, xs_set)
            for c in range(NC):
                xw = Count(act, x_in[c])
                act.wait_ge(x_in[c], xw.up(16))
                act.activation(ntmp[:, :, :], fz[:, 0:KB, c * CH:(c + 1) * CH], ACT.Square).then_inc(sq_set, 1)
                root(c)
                if c:
                    act.wait_ge(xs_set, xs.up(1))
                    act.activation(rx[:, 0:KB, (c - 1) * CH:c * CH], fz[:, 0:KB, (c - 1) * CH:c * CH], ACT.Copy)\
                        .then_inc(nhi, 1)
            act.wait_ge(xs_set, xs.up(1))
            act.activation(rx[:, 0:KB, 2 * CH:3 * CH], fz[:, 0:KB, 2 * CH:3 * CH], ACT.Copy).then_inc(nhi, 1)

            r_i, r_f, r_t = cacc, csum, glub
            act.wait_ge(const_in, cin.up(64))
            for c in range(NC):
                cols = slice(c * CH, (c + 1) * CH)
                act.wait_ge(tbank_full, full.up(1))
                evac(r_i[0:NH, cols], bias=gpar[:, 0:1], rows_=slice(0, NH)).then_inc(gate_row, 1)
                evac(r_f[0:NH, cols], bias=gpar[:, 1:2], rows_=slice(32, 32 + NH)).then_inc(tbank_free, 1)
                n["t"] += 1
            gr = Count(act, gate_row)
            tf = Count(act, tbank_free)
            act.wait_ge(tbank_free, tf.up(3))
            gd = Count(act, gate_dve)
            act.activation(r_t[0:NH, 0:T], r_f[0:NH, :], ACT.Abs).then_inc(gate_row, 1)
            act.wait_ge(gate_row, gr.up(4))
            act.activation(r_t[0:NH, 0:T], r_t[0:NH, 0:T], ACT.Exp, scale=-1.0).then_inc(gate_row, 1)
            act.wait_ge(gate_row, gr.up(1))
            act.activation(r_t[0:NH, 0:T], r_t[0:NH, 0:T], ACT.Ln, bias=1.0).then_inc(gate_row, 1)
            act.wait_ge(gate_dve, gd.up(9))
            act.activation(g4[32:32 + NH, 0:T], r_t[0:NH, 0:T], ACT.Exp).then_inc(gate_row, 1)
            act.activation(g4[64:64 + NH, 0:T], row3[0:NH, :], ACT.Exp, scale=-1.0).then_inc(gate_row, 1)
            act.activation(g4[96:96 + NH, 0:T], r_i[0:NH, :], ACT.Exp).then_inc(gate_row, 1)

            sf = Count(act, stab_free)
            so = [Count(act, spl_out[s]) for s in range(2)]
            ms.up(0)
            with repeat(act, KB, full, sf, *so) as i:
                act.wait_ge(stab_free, sf.up(2))
                evac_tile(sta)
                evac_tile(stb, ACT.Sigmoid)
                for j, (func, scale) in enumerate(((ACT.Identity, 1.0), (ACT.Identity, DH ** -0.5),
                                                   (ACT.Identity, 1.0), (ACT.Sigmoid, 1.0))):
                    act.wait_ge(spl_out[j % 2], so[j % 2].up(16))
                    evac_tile(spl[j % 2], func, 0.0, scale)
            muw = Count(act, mu_full)
            mus = Count(act, mu_set)

            def gate_a(i, pos, half):
                act.wait_ge(spl_out[pos], so[pos].up(16))
                evac_tile(spl[pos], ACT.Sigmoid, pars[:, bass.ds(i * 2 + (PV["bga"] + pos + half * KB // 2), 1)])

            for c in range(NC):
                act.wait_ge(mu_full, muw.up(1))
                act.activation(sta[:, c * CH:(c + 1) * CH], bank(2 + c, 0, CH), ACT.Copy, scale=1.0 / D)\
                    .then_inc(mu_set, 1)
            with repeat(act, KB // 4, full, *so, ahead=[(full, 1)]) as i:
                for pos in range(2):
                    gate_a(i, pos, 0)
            for c in range(NC):
                cols = slice(c * CH, (c + 1) * CH)
                act.wait_ge(mu_full, muw.up(1))
                act.activation(sta[:, cols], bank(2 + c, 0, CH), ACT.Ln, bias=eps[:, 0:1], scale=1.0 / D)\
                    .then_inc(mu_set, 1)
            act.wait_ge(mu_set, mus.up(6))
            act.activation(sta[:, :], sta[:, :], ACT.Exp, scale=-0.5).then_inc(mu_set, 1)
            cn = Count(act, cn_set, start=CN_SQ)
            with repeat(act, KB // 4, full, cn, *so, ahead=[(full, 1), (cn, 1)]) as i:
                for pos in range(2):
                    for j in range(2):
                        k = i * 4 + (2 * pos + j)
                        act.wait_ge(cn_set, cn.up(1))
                        settle(cn, 2)
                        act.activation(glub[:, 0:T], stb[:, :], ACT.Sigmoid,
                                       bias=pars[:, bass.ds(k + PV["lnb"], 1)],
                                       scale=pars[:, bass.ds(k + PV["lng"], 1)]).then_inc(csig, 1)
                        act.wait_ge(cn_set, cn.up(2))
                        settle(cn)
                        act.activation(block_of(rz, k), stb[:, :], ACT.Copy).then_inc(chi, 1)
                    gate_a(i, pos, 1)

            qin = Count(act, qkv_in)
            kvw = Count(act, kv_full)
            wn = Count(act, wneg)
            a3 = Count(act, a32)
            nf = Count(act, n_full)
            hw = Count(act, hn_set)
            ds = Count(act, dsm)
            vg = Count(act, vlog)
            cg = Count(act, cahi)
            sq_own = Count(act, ssq)
            mbo = Count(act, mixb_out)
            mbs = Count(act, mixb)

            def split_qk(h):
                act.wait_ge(qkv_in, qin.up(32))
                act.activation(qkh[h % 2][:, :, :, :], qkv[:, :, 0:2, :], ACT.Copy).then_inc(qkhi, 1)

            def after_scores(h):
                act.wait_ge(kv_full, kvw.up(1))
                act.activation(vh[:, 0:DH], bank(2, 2 * P, DH), ACT.Copy).then_inc(vkhi, 1)
                act.activation(kh[:, :], bank(2, 0, DH), ACT.Copy, scale=gtc[:, 12 + h:13 + h]).then_inc(vkhi, 1)
                act.wait_ge(wneg, wn.up(1))
                act.activation(wt[:, :], wt[:, :], ACT.Exp).then_inc(wexp, 1)
                act.activation(ch[:, :, :], c32[:, h, :, :], ACT.Copy).then_inc(cahi, 1)
                act.wait_ge(a32, a3.up(1))
                act.activation(ah[:, :], wt[:, :], ACT.Copy).then_inc(cahi, 1)

            def after_values(h):
                act.wait_ge(n_full, nf.up(1))
                act.activation(hn[:, :], bank(5, 0, VW), ACT.Copy, scale=gtc[:, 4 + h:5 + h]).then_inc(t1_set, 1)
                act.wait_ge(hn_set, hw.up(1))
                act.activation(zt[:, :], hn[:, 0:DH], ACT.Square, accum_out=sm[:, 3:4]).then_inc(ssq, 1)
                act.wait_ge(dsm, ds.up(4))
                act.activation(sm[:, 5:6], sm[:, 4:5], ACT.Ln, bias=eps[:, 0:1], scale=1.0 / DH).then_inc(vlog, 1)
                act.wait_ge(vlog, vg.up(1))
                act.activation(sm[:, 6:7], sm[:, 5:6], ACT.Exp, scale=-0.5).then_inc(rs_set, 1)

            def mlstm(go):
                split_qk(0), go()
                after_scores(0), split_qk(1), go()
                after_values(0), after_scores(1), split_qk(2), go()
                after_values(1), after_scores(2), split_qk(3), go()
                after_values(2), after_scores(3), go()
                after_values(3), go()

            cbw = Count(act, clo_b)
            act.wait_ge(clo_b, cbw.up(KB + 1))
            for s in range(2):
                so[s].up(16)
                act.wait_ge(spl_out[s], so[s].now())
            with repeat(act, NCHUNK, full, qin, kvw, wn, a3, nf, hw, ds, vg, mbo, mbs, ahead=[(full, 1)]) as i:
                def steps():
                    act.wait_ge(mixb_out, mbo.up(16))
                    for c in range(NC):
                        act.wait_ge(tbank_full, full.up(1))
                        settle(full)
                        evac(sigb[:, c * CH:(c + 1) * CH], ACT.Exp, nbgb[:, bass.ds(i, 1)], -1.0).then_inc(tbank_free, 1)
                        n["t"] += 1
                        yield
                    for c in range(NC):
                        if c:
                            full.up(1), mbs.up(1)
                            act.wait_ge(tbank_full, full.now())
                            act.wait_ge(mixb, mbs.now())
                        else:
                            act.wait_ge(tbank_full, full.up(1))
                        settle(full)
                        evac(ybs[:, :], ACT.Identity, pars[:, bass.ds(i + PV["bpb"], 1)]).then_inc(tbank_free, 1)
                        n["t"] += 1
                        yield
                    
                it = steps()
                mlstm(lambda: next(it))
                mbs.up(1)
                assert next(it, "end") == "end"
            cld = Count(act, c_ld)
            act.wait_ge(c_ld, cld.up(16))
            mlstm(lambda: None)

            zin = [Count(act, zl_in[s]) for s in range(2)]
            for k in range(KB):
                act.wait_ge(zl_in[k % 2], zin[k % 2].up(16))
                act.activation(rx[:, k, :], zl[k % 2][:, :], ACT.Copy).then_inc(zhi, 1)
            mxs = Count(act, mix_step)
            mxl = Count(act, mixlo)
            yl = Count(act, mixlo, start=-2)
            evac_first = [0]
            yl.up(2)
            for m in range(KB):
                if m >= 2:
                    yl.up(1)
                    if yl.due():
                        act.wait_ge(mixlo, yl.now())
                evac_tile(yas[m % 2])
                act.wait_ge(mix_step, mxs.up(2))
                act.activation(rz[:, m, :], yas[m % 2][:, :], ACT.Copy).then_inc(mixhi, 1)
            osw = Count(act, oss_set, start=1 - 2)
            for m in range(KB):
                for c in range(NC):
                    j = 3 * m + c
                    full.up(1), osw.up(1)
                    act.wait_ge(tbank_full, full.now())
                    if osw.due():
                        act.wait_ge(oss_set, osw.now())
                    b = n["t"] % 2
                    act.activation(osq[j % 2][:, :], bank(b, 0, CH), ACT.Square).then_inc(osq_set, 1)
                    evac(fx[:, m, c * CH:(c + 1) * CH], ACT.Copy, 0.0,
                         pars[:, PV["post"] + m:PV["post"] + m + 1]).then_inc(tbank_free, 1)
                    n["t"] += 1
            for c in range(NC):
                root(c)
            x1w = Count(act, x1_set)
            x1gw = Count(act, x1g)
            for c in range(NC):
                cols = slice(c * CH, (c + 1) * CH)
                act.wait_ge(x1_set, x1w.up(1))
                act.activation(ntmp[:, :, :], fx[:, KB:2 * KB, cols], ACT.Square).then_inc(sq_set, 1)
                for k in range(KB):
                    act.activation(fx[:, k, cols], fx[:, KB + k, cols], ACT.Copy,
                                   scale=pars[:, PV["fpre"] + k:PV["fpre"] + k + 1]).then_inc(x1g, 1)
                root(c)
                act.wait_ge(xs_set, xs.up(1))
                act.activation(rz[:, 0:KB, cols], fx[:, 0:KB, cols], ACT.Copy).then_inc(nhi, 1)

            fd = Count(act, conv_set, start=-2)
            cvw = Count(act, conv_set)
            g3 = Count(act, g32)
            dbw = Count(act, dbank_full)
            hz = Count(act, fdv)
            nlw = Count(act, nlo)
            nlw.up(2 * NC), hz.up(2)
            act.wait_ge(nlo, nlw.now())
            act.wait_ge(fdv, hz.now())

            def up_a():
                fd.up(1)
                if fd.due():
                    act.wait_ge(conv_set, fd.now())
                evac_tile(ub[0], off=2)
                act.wait_ge(conv_set, cvw.up(1))
                act.activation(cv[0][:, :], cv[0][:, :], ACT.Gelu_apprx_tanh).then_inc(gelu_set, 1)

            def up_b(j, first):
                fd.up(1)
                if fd.due():
                    act.wait_ge(conv_set, fd.now())
                evac_tile(ub[1], off=2)
                cvw.up(1)
                g3.up(1), dbw.up(24 if first else 0)
                act.wait_ge(g32, g3.now())
                act.wait_ge(dbank_full, dbw.now())
                act.activation(rg[:, j, :], cv[0][:, :], ACT.Copy).then_inc(ghi, 1)

            def turn(par, last=False):
                up_a(), up_b(2 * (1 - par) + 1, False)
                if not last:
                    up_a(), up_b(2 * par, True)

            for j in range(3):
                up_a(), up_b(j, False)
            turn(0)
            with repeat(act, (NG - 3) // 2, full, fd, cvw, g3, dbw) as i:
                turn(1)
                turn(0)
            turn(1, last=True)
            df = Count(act, dbank_free)
            act.wait_ge(dbank_free, df.up(24 * NG))
            for c in range(NC):
                act.activation(ntmp[:, :, :], fx[:, KB:2 * KB, c * CH:(c + 1) * CH], ACT.Square).then_inc(sq_set, 1)
                root(c)

        @block.vector
        def _(dve):
            rw = Count(dve, r_set)
            hiw = Count(dve, nhi)
            cin = Count(dve, const_in)
            cst = Count(dve, const_set)
            cin.up(64), cst.up(9)
            dve.wait_ge(const_in, cin.now())
            dve.wait_ge(const_set, cst.now())
            for c in range(NC):
                cols = slice(c * CH, (c + 1) * CH)
                dve.wait_ge(r_set, rw.up(1))
                for k in range(KB):
                    op = dve.scalar_tensor_tensor(fz[:, k, cols], fz[:, k, cols], pars[:, PV["pre"] + k:PV["pre"] + k + 1],
                                                  rst[c][:, :], ALU.mult, ALU.mult)
                op.then_inc(xs_set, 1)
                dve.wait_ge(nhi, hiw.up(1))
                dve.tensor_tensor(rx[:, KB:2 * KB, cols], fz[:, 0:KB, cols], rx[:, 0:KB, cols].bitcast(F32),
                                  ALU.subtract).then_inc(nlo, 1)
            gd = Count(dve, gate_dve)
            gr = Count(dve, gate_row)
            r_i, r_f, r_t = cacc, csum, glub

            def own(k=1):
                dve.wait_ge(gate_dve, gd.up(k))

            dve.memset(row3[0:NH, :], 1.0).then_inc(gate_dve, 1)
            own()
            dve.memset(row3[0:NH, 0:SEQ:L], 0.0).then_inc(gate_dve, 1)
            dve.memset(row3[0:NH, S0:S0 + 1], 0.0).then_inc(gate_dve, 1)
            gr.up(6), gd.up(2)
            dve.wait_ge(gate_row, gr.now())
            dve.wait_ge(gate_dve, gd.now())
            dve.scalar_tensor_tensor(r_f[0:NH, :], r_f[0:NH, :], 0.0, r_t[0:NH, 0:T], ALU.min, ALU.subtract)\
                .then_inc(gate_dve, 1)
            own()
            dve.tensor_tensor_scan(r_t[0:NH, 0:T], row3[0:NH, :], r_f[0:NH, :], 0.0, ALU.mult, ALU.add)\
                .then_inc(gate_dve, 1)
            own()
            dve.tensor_tensor_scan(row3[0:NH, 0:S0], r_f[0:NH, 0:S0], r_i[0:NH, 0:S0], 0.0, ALU.add, ALU.max)\
                .then_inc(gate_dve, 1)
            dve.tensor_tensor_scan(row3[0:NH, S0:T], r_f[0:NH, S0:T], r_i[0:NH, S0:T], gpar[:, 2:3],
                                   ALU.add, ALU.max).then_inc(gate_dve, 1)
            own(2)
            dve.memset(g4[:, :], 0.0).then_inc(cdv0, 1)
            dve.wait_ge(cdv0, 1)
            dve.memset(g4[64:96, :], 1.0).then_inc(cdv0, 1)
            dve.tensor_tensor(g4[0:NH, 0:T], r_i[0:NH, :], r_t[0:NH, 0:T], ALU.subtract).then_inc(cdv0, 1)
            dve.tensor_tensor(r_f[0:NH, :], row3[0:NH, :], r_t[0:NH, 0:T], ALU.subtract).then_inc(cdv0, 1)
            dve.wait_ge(cdv0, 4)
            lastM = r_f[0:NH, L - 1:SEQ:L]
            dve.tensor_tensor(r_i[0:NH, 0:SEQ].rearrange("h (c l) -> h c l", l=L),
                              g4[0:NH, 0:SEQ].rearrange("h (c l) -> h c l", l=L),
                              lastM.unsqueeze(2).broadcast_to([NH, NCHUNK, L]), ALU.subtract).then_inc(cdv0, 1)
            dve.tensor_scalar(r_i[0:NH, S0:T], g4[0:NH, S0:T], r_f[0:NH, T - 1:T], None, ALU.subtract)\
                .then_inc(cdv0, 1)
            dve.tensor_scalar(r_t[0:NH, 0:L], r_f[0:NH, 0:L], -1.0, None, ALU.mult).then_inc(cdv0, 1)
            before = row3[0:NH, L - 1:SEQ - 1:L]
            dve.tensor_tensor(r_t[0:NH, L:SEQ].rearrange("h (c l) -> h c l", l=L),
                              before.unsqueeze(2).broadcast_to([NH, NCHUNK - 1, L]),
                              r_f[0:NH, L:SEQ].rearrange("h (c l) -> h c l", l=L), ALU.subtract)\
                .then_inc(gate_dve, 1)
            dve.tensor_scalar(r_t[0:NH, S0:T], r_f[0:NH, S0:T], -1.0, gpar[:, 2:3], ALU.mult, ALU.add)\
                .then_inc(gate_dve, 1)
            dve.wait_ge(cdv0, 7)
            own(2)
            dve.tensor_scalar(r_f[0:NH, :], r_f[0:NH, :], -1.0, None, ALU.mult).then_inc(gate_dve, 1)
            dve.tensor_copy(mouts[:, 0:1], row3[0:NH, SEQ - 1:SEQ]).then_inc(cdv0, 1)
            dve.tensor_copy(mouts[:, 1:2], row3[0:NH, T - 1:T]).then_inc(gate_dve, 1)
            dve.wait_ge(gate_row, gr.up(3))
            dve.tensor_copy(drow[:, 0:NCHUNK], g4[32:32 + NH, L - 1:SEQ:L]).then_inc(cdv0, 1)
            dve.tensor_copy(drow[:, NCHUNK:NCHUNK + 1], g4[32:32 + NH, T - 1:T]).then_inc(gate_dve, 1)
            dve.tensor_scalar(nbgb[:, :], pars[:, PV["bgb"]:PV["bgb"] + KB], -1.0, None, ALU.mult).then_inc(cdv0, 1)
            nlw = Count(dve, nlo)
            dve.wait_ge(nlo, nlw.up(NC))
            dve.memset(fz[:, KB:2 * KB, SEQ:S0], 0.0).then_inc(cdv0, 1)
            no = Count(dve, neg_out)
            dve.wait_ge(neg_out, no.up(16))
            dve.memset(csum[:, :], 0.0).then_inc(cdv0, 1)
            dve.memset(cacc[:, SEQ:S0], 0.0).then_inc(cdv0, 1)
            dve.memset(glub[:, 0:HALO], 0.0).then_inc(cdv0, 1)
            dve.wait_ge(cdv0, 14)
            dve.memset(ctail[:, 0:1], 0.0).then_inc(stab_free, 2)

            tf = Count(dve, tbank_free, start=3)
            cd = Count(dve, cdv)
            seg = ((GP0, SEQ, 0), (GS0, DEC, S0))
            stw = Count(dve, stab_free, start=2)
            with repeat(dve, KB, tf, cd, stw) as i:
                dve.tensor_copy(wcur[:, 0:CW], pars[:, bass.ds(i * CW + PDW, CW)]).then_inc(cdv, 1)
                dve.tensor_copy(wcur[:, CW:CW + 1], pars[:, bass.ds(i + PV["convb"], 1)]).then_inc(cdv, 1)
                dve.tensor_copy(glub[:, GS0 - HALO:GS0], chalo[:, bass.ds(i * HALO, HALO)]).then_inc(cdv, 1)
                dve.wait_ge(tbank_free, tf.up(6))
                for at, w, t0 in seg:
                    op = dve.tensor_tensor(glub[:, at:at + w], sta[:, t0:t0 + w], stb[:, t0:t0 + w], ALU.mult)
                    op.then_inc(cdv, 1) if t0 == 0 else op.then_inc(stab_free, 2)
                cd.up(4), stw.up(2)
                dve.wait_ge(cdv, cd.now())
                dve.wait_ge(stab_free, stw.now())
                for j in range(CW):
                    for at, w, t0 in seg:
                        if j:
                            dve.wait_ge(cdv, cd.up(1))
                        src = glub[:, at - HALO + j:at - HALO + j + w]
                        acc = cacc[:, t0:t0 + w]
                        if j == 0:
                            dve.tensor_scalar(acc, src, wcur[:, 0:1], wcur[:, CW:CW + 1], ALU.mult, ALU.add)\
                                .then_inc(cdv, 1)
                        else:
                            dve.scalar_tensor_tensor(acc, src, wcur[:, j:j + 1], acc, ALU.mult, ALU.add)\
                                .then_inc(cdv, 1)
                dve.wait_ge(cdv, cd.up(2))
                dve.tensor_copy(block_of(fz, i + KB), cacc[:, :]).then_inc(cdv, 1)
                dve.tensor_tensor(csum[:, :], csum[:, :], cacc[:, :], ALU.add).then_inc(cdv, 1)
                dve.tensor_copy(ctail[:, bass.ds(i * (2 * HALO), HALO)], glub[:, GP0 + SEQ - HALO:GP0 + SEQ]).then_inc(cdv, 1)
                dve.tensor_copy(ctail[:, bass.ds(i * (2 * HALO) + HALO, HALO)], glub[:, GW - HALO:GW]).then_inc(cdv, 1)
                dve.wait_ge(cdv, cd.up(4))
                tf.up(12)

            g4w = Count(dve, g4_t)
            dve.wait_ge(g4_t, g4w.up(1))
            cols9 = ps[:, 5 * 512:5 * 512 + (NCHUNK + 1) * P].rearrange("p (c t q) -> p c t q", t=4, q=32)
            dve.tensor_copy(gt[:, :].rearrange("p (c t h) -> p c t h", t=4, h=NH), cols9[:, :, :, 0:NH])\
                .then_inc(gt_set, 1)
            dve.tensor_copy(decs[:, :, :], bank(7, 256, 16 * NH).rearrange("p (h c) -> p h c", c=16)[:, :, 0:NCHUNK + 1])\
                .then_inc(gt_set, 1)
            mus = Count(dve, mu_set)
            cn = Count(dve, cn_set)
            dve.memset(csq[:, :], 0.0).then_inc(cn_set, 1)
            mus.up(3), cn.up(1)
            dve.wait_ge(mu_set, mus.now())
            dve.wait_ge(cn_set, cn.now())
            with repeat(dve, KB, cn) as i:
                ck = block_of(fz, i + KB)
                dve.tensor_tensor(ck, ck, sta[:, :], ALU.subtract).then_inc(cn_set, 1)
                dve.wait_ge(cn_set, cn.up(1))
                dve.tensor_tensor(sqt[:, :], ck, ck, ALU.mult).then_inc(cn_set, 1)
                dve.wait_ge(cn_set, cn.up(1))
                dve.tensor_tensor(csq[:, :], csq[:, :], sqt[:, :], ALU.add).then_inc(cn_set, 1)
                dve.wait_ge(cn_set, cn.up(1))
            sg = Count(dve, csig)
            chw = Count(dve, chi)
            clw = Count(dve, clo_b)
            dve.wait_ge(mu_set, mus.up(4))
            with repeat(dve, KB, cn, sg, chw, clw) as i:
                dve.tensor_tensor(stb[:, :], block_of(fz, i + KB), sta[:, :], ALU.mult).then_inc(cn_set, 1)
                sg.up(1), cn.up(1)
                dve.wait_ge(csig, sg.now())
                dve.wait_ge(cn_set, cn.now())
                dve.tensor_scalar(stb[:, :], stb[:, :], pars[:, bass.ds(i + PV["lng"], 1)],
                                  pars[:, bass.ds(i + PV["lnb"], 1)], ALU.mult, ALU.add).then_inc(cn_set, 1)
                dve.wait_ge(cn_set, cn.up(1))
                dve.tensor_tensor(stb[:, :], stb[:, :], glub[:, 0:T], ALU.mult).then_inc(cn_set, 1)
                chw.up(1), cn.up(1)
                dve.wait_ge(chi, chw.now())
                dve.wait_ge(cn_set, cn.now())
                dve.tensor_tensor(block_of(rz, i + KB), stb[:, :], block_of(rz, i).bitcast(F32), ALU.subtract)\
                    .then_inc(clo_b, 1)
                dve.wait_ge(clo_b, clw.up(1))

            so = [Count(dve, spl_out[s]) for s in range(2)]
            to = Count(dve, tail_out)
            for s in range(2):
                dve.wait_ge(spl_out[s], so[s].up(16 * (1 + 2 * KB + KB // 2)))
            dve.wait_ge(tail_out, to.up(64))
            dve.memset(c32[:, :, :, :], 0.0).then_inc(gt_set, 1)
            for part, value in ((vh[:, DH:DH + 1], 1.0), (vh[:, DH + 1:VW], 0.0), (vl[:, DH:VW], 0.0)):
                dve.memset(part.bitcast(F32), value).then_inc(gt_set, 1)
            dve.memset(sm[:, :], 0.0).then_inc(clo_b, 1)
            tf.up(3 * KB)
            gts = Count(dve, gt_set)
            gts.up(6), clw.up(1)
            dve.wait_ge(gt_set, gts.now())
            dve.wait_ge(clo_b, clw.now())
            ni = Count(dve, neg_in)
            gtw = Count(dve, gtc_set)
            qh = Count(dve, qkhi)
            sf = Count(dve, s_full)
            vk = Count(dve, vkhi)
            we = Count(dve, wexp)
            ca = Count(dve, cahi)
            t1 = Count(dve, t1_set)
            hnw = Count(dve, hn_set)
            ds = Count(dve, dsm)
            sq = Count(dve, ssq)
            rs = Count(dve, rs_set)
            zf = Count(dve, z_full)
            oi = Count(dve, o_in)
            zo = Count(dve, z_out)
            st = Count(dve, sig_step)

            def split_qk(h):
                dve.wait_ge(qkhi, qh.up(1))
                dve.tensor_tensor(qkl[h % 2][:, :, :, :], qkv[:, :, 0:2, :], qkh[h % 2][:, :, :, :].bitcast(F32),
                                  ALU.subtract).then_inc(qklo, 1)

            def after_scores(h):
                dve.wait_ge(s_full, sf.up(1))
                dve.scalar_tensor_tensor(wt[:, :], bank(3, 0, L), gtc[:, h:h + 1], mask[:, :], ALU.add, ALU.min)\
                    .then_inc(wneg, 1)
                dve.wait_ge(vkhi, vk.up(2))
                dve.tensor_tensor(vl[:, 0:DH], bank(2, 2 * P, DH), vh[:, 0:DH].bitcast(F32), ALU.subtract)\
                    .then_inc(kvlo, 1)
                dve.scalar_tensor_tensor(kl[:, :], bank(2, 0, DH), gtc[:, 12 + h:13 + h], kh[:, :].bitcast(F32),
                                         ALU.mult, ALU.subtract).then_inc(kvlo, 1)
                dve.wait_ge(wexp, we.up(1))
                dve.tensor_tensor(wt[:, :], bank(3, L, L), wt[:, :], ALU.mult).then_inc(a32, 1)
                dve.wait_ge(cahi, ca.up(2))
                dve.tensor_tensor(cl[:, :, :], c32[:, h, :, :], ch[:, :, :].bitcast(F32), ALU.subtract)\
                    .then_inc(kvlo, 1)
                dve.tensor_tensor(al[:, :], wt[:, :], ah[:, :].bitcast(F32), ALU.subtract).then_inc(alo, 1)

            def after_values(h):
                dve.wait_ge(t1_set, t1.up(1))
                dve.tensor_tensor(hn[:, :], bank(4, 0, VW), hn[:, :], ALU.add).then_inc(hn_set, 1)
                dve.wait_ge(hn_set, hnw.up(1))
                den = hn[:, DH:DH + 1]
                dve.scalar_tensor_tensor(sm[:, 0:1], den, -1.0, den, ALU.mult, ALU.max).then_inc(dsm, 1)
                dve.wait_ge(dsm, ds.up(1))
                dve.tensor_tensor(sm[:, 1:2], sm[:, 0:1], gtc[:, 8 + h:9 + h], ALU.max).then_inc(dsm, 1)
                dve.wait_ge(dsm, ds.up(1))
                dve.reciprocal(sm[:, 2:3], sm[:, 1:2]).then_inc(dsm, 1)
                ds.up(1), sq.up(1)
                dve.wait_ge(dsm, ds.now())
                dve.wait_ge(ssq, sq.now())
                dve.tensor_scalar(sm[:, 4:5], sm[:, 3:4], sm[:, 2:3], sm[:, 2:3], ALU.mult, ALU.mult)\
                    .then_inc(dsm, 1)
                ds.up(1)
                for b in range(2):
                    dve.scalar_tensor_tensor(c32[:, h, b, :], c32[:, h, b, :], dcc[:, h:h + 1], bank(6 + b, 0, VW),
                                             ALU.mult, ALU.add).then_inc(cupd, 1)
                dve.wait_ge(rs_set, rs.up(1))
                dve.tensor_scalar(zt[:, :], hn[:, 0:DH], sm[:, 2:3], sm[:, 6:7], ALU.mult, ALU.mult)\
                    .then_inc(zt_set, 1)

            def rows_out(h):
                zf.up(1), oi.up(32), zo.up(16)
                dve.wait_ge(z_full, zf.now())
                dve.wait_ge(o_in, oi.now())
                dve.wait_ge(z_out, zo.now())
                for b in range(2):
                    g = PV["mnorm"] + 2 * h + b
                    dve.scalar_tensor_tensor(zs[:, b, :], bank(3, 256 + b * L, L), pars[:, g:g + 1], ob[:, b, :],
                                             ALU.mult, ALU.mult).then_inc(zs_set, 1)

            def mlstm(c, go):
                dve.tensor_copy(gtc[:, :], gt[:, bass.ds(c * 16, 16)]).then_inc(gtc_set, 1)
                dve.tensor_copy(dcc[:, :], decs[:, :, bass.ds(c, 1)]).then_inc(gtc_set, 1)
                ni.up(16), gtw.up(2)
                dve.wait_ge(neg_in, ni.now())
                dve.wait_ge(gtc_set, gtw.now())
                split_qk(0), go()
                after_scores(0), split_qk(1), go()
                after_values(0), after_scores(1), split_qk(2), go()
                rows_out(0), after_values(1), after_scores(2), split_qk(3), go()
                rows_out(1), after_values(2), after_scores(3), go()
                rows_out(2), after_values(3), go()
                rows_out(3)

            with repeat(dve, NCHUNK, tf, ni, gtw, qh, sf, vk, we, ca, t1, hnw, ds, sq, rs, zf, oi, zo, st) as i:
                def steps():
                    for c in range(NC):
                        cols = slice(c * CH, (c + 1) * CH)
                        dve.wait_ge(tbank_free, tf.up(1))
                        dve.tensor_scalar(sigb[:, cols], sigb[:, cols], 1.0, None, ALU.add).then_inc(sig_step, 1)
                        dve.wait_ge(sig_step, st.up(2 if c else 1))
                        dve.reciprocal(sigb[:, cols], sigb[:, cols]).then_inc(sig_step, 1)
                        yield
                    for c in range(NC):
                        cols = slice(c * CH, (c + 1) * CH)
                        if c == 0:
                            st.up(1)
                        dve.wait_ge(tbank_free, tf.up(1))
                        if c == 0:
                            dve.wait_ge(sig_step, st.now())
                        dve.tensor_tensor(sigb[:, cols], sigb[:, cols], ybs[:, :], ALU.mult).then_inc(mixb, 1)
                        yield
                it = steps()
                mlstm(i, lambda: next(it))
                assert next(it, "end") == "end"
            mlstm(NCHUNK, lambda: None)

            zh = Count(dve, zhi)
            for k in range(KB):
                dve.wait_ge(zhi, zh.up(1))
                dve.tensor_tensor(rx[:, KB + k, :], zl[k % 2][:, :], rx[:, k, :].bitcast(F32), ALU.subtract)\
                    .then_inc(zlo, 1)
            gi = [Count(dve, ga_in[s]) for s in range(2)]
            mi = [Count(dve, mb_in[s]) for s in range(2)]
            mxs = Count(dve, mix_step)
            mh = Count(dve, mixhi)
            for m in range(KB):
                s = m % 2
                tf.up(3), gi[s].up(16)
                dve.wait_ge(tbank_free, tf.now())
                dve.wait_ge(ga_in[s], gi[s].now())
                dve.tensor_tensor(yas[s][:, :], yas[s][:, :], gal[s][:, :], ALU.mult).then_inc(mix_step, 1)
                mxs.up(1), mi[s].up(16)
                dve.wait_ge(mix_step, mxs.now())
                dve.wait_ge(mb_in[s], mi[s].now())
                dve.tensor_tensor(yas[s][:, :], yas[s][:, :], mbl[s][:, :], ALU.add).then_inc(mix_step, 1)
                mxs.up(1)
                dve.wait_ge(mixhi, mh.up(1))
                dve.tensor_tensor(rz[:, KB + m, :], yas[s][:, :], rz[:, m, :].bitcast(F32), ALU.subtract)\
                    .then_inc(mixlo, 1)
            oq = Count(dve, osq_set)
            os_ = Count(dve, oss_set)
            dve.memset(oss[:, :], 0.0).then_inc(oss_set, 1)
            for j in range(NC * KB):
                cols = slice(j % NC * CH, (j % NC + 1) * CH)
                oq.up(1), os_.up(1)
                dve.wait_ge(osq_set, oq.now())
                dve.wait_ge(oss_set, os_.now())
                dve.tensor_tensor(oss[:, cols], oss[:, cols], osq[j % 2][:, :], ALU.add).then_inc(oss_set, 1)
            ow = Count(dve, orr)
            xg = Count(dve, x1g)

            def root_of(c):
                return rst[c][:, :].unsqueeze(1).broadcast_to([P, KB, CH])

            def residual(c):
                cols = slice(c * CH, (c + 1) * CH)
                xin = Count(dve, x_in[c], start=16)
                rw.up(1), xin.up(16)
                dve.wait_ge(r_set, rw.now())
                dve.wait_ge(x_in[c], xin.now())
                dve.tensor_tensor(fx[:, 0:KB, cols], fx[:, 0:KB, cols], root_of(c), ALU.mult).then_inc(orr, 1)
                dve.wait_ge(orr, ow.up(1))
                dve.tensor_tensor(fx[:, KB:2 * KB, cols], fx[:, KB:2 * KB, cols], fx[:, 0:KB, cols], ALU.add)\
                    .then_inc(x1_set, 1)

            def normed(c):
                cols = slice(c * CH, (c + 1) * CH)
                rw.up(1), xg.up(KB)
                dve.wait_ge(r_set, rw.now())
                dve.wait_ge(x1g, xg.now())
                dve.tensor_tensor(fx[:, 0:KB, cols], fx[:, 0:KB, cols], root_of(c), ALU.mult).then_inc(xs_set, 1)
                dve.wait_ge(nhi, hiw.up(1))
                dve.tensor_tensor(rz[:, KB:2 * KB, cols], fx[:, 0:KB, cols], rz[:, 0:KB, cols].bitcast(F32),
                                  ALU.subtract).then_inc(nlo, 1)

            for c in range(NC):
                residual(c)
            for c in range(NC):
                normed(c)

            nlw = Count(dve, nlo)
            fd = Count(dve, fdv)
            dve.wait_ge(nlo, nlw.up(2 * NC))
            for s in range(2):
                dve.memset(ub[s][:, 0:2], 0.0).then_inc(fdv, 1)
            x1o = Count(dve, x1_out)
            fd.up(2), x1o.up(16 * NC)
            dve.wait_ge(fdv, fd.now())
            dve.wait_ge(x1_out, x1o.now())
            tf.up(3 * KB)
            cs = Count(dve, conv_step)
            cw = Count(dve, conv_set)
            ge = Count(dve, gelu_set)
            g3 = Count(dve, g32)
            gh = Count(dve, ghi)
            df = Count(dve, dbank_full)
            dfo = Count(dve, dbank_free, start=-24)

            def conv(s, tile_):
                dve.wait_ge(tbank_free, tf.up(3))
                dve.tensor_copy(fcur[:, :], pars[:, bass.ds(tile_ * 4 + PFF, 4)]).then_inc(fdv, 1)
                dve.tensor_copy(ub[s][:, S0:S0 + 2], fhalo[:, bass.ds(tile_ * 2, 2)]).then_inc(fdv, 1)
                gap = T - SEQ
                tails = ub[s][:, T + 2 - 2 * gap:T + 2].rearrange("p (g n) -> p g n", g=2)[:, :, gap - 2:gap]
                dve.tensor_copy(ftail[:, bass.ds(tile_ * 4, 4)].rearrange("p (g n) -> p g n", g=2), tails)\
                    .then_inc(fdv, 1)
                dve.wait_ge(fdv, fd.up(3))
                dve.tensor_scalar(cv[s][:, :], ub[s][:, 2:T + 2], fcur[:, 2:3], fcur[:, 3:4], ALU.mult, ALU.add)\
                    .then_inc(conv_step, 1)
                dve.wait_ge(conv_step, cs.up(1))
                dve.scalar_tensor_tensor(cv[s][:, :], ub[s][:, 1:T + 1], fcur[:, 1:2], cv[s][:, :],
                                         ALU.mult, ALU.add).then_inc(conv_step, 1)
                dve.wait_ge(conv_step, cs.up(1))
                dve.scalar_tensor_tensor(cv[s][:, :], ub[s][:, 0:T], fcur[:, 0:1], cv[s][:, :],
                                         ALU.mult, ALU.add).then_inc(conv_set, 1)
                cw.up(1)

            def ff_block(j, b2):
                conv(0, b2)
                conv(1, b2 + 1)
                ge.up(1), cw.up(0)
                dve.wait_ge(gelu_set, ge.now())
                dve.wait_ge(conv_set, cw.now())
                dve.tensor_tensor(cv[0][:, :], cv[0][:, :], cv[1][:, :], ALU.mult).then_inc(g32, 1)
                gh.up(1), g3.up(1)
                dve.wait_ge(ghi, gh.now())
                dve.wait_ge(g32, g3.now())
                dve.tensor_tensor(rg[:, 4 + j, :], cv[0][:, :], rg[:, j, :].bitcast(F32), ALU.subtract)\
                    .then_inc(glo, 1)

            def add_down(half, first):
                dfo.up(12)
                if dfo.due():
                    dve.wait_ge(dbank_free, dfo.now())
                for m in range(4 * half, 4 * half + 4):
                    for c in range(NC):
                        f = fx[:, KB + m, c * CH:(c + 1) * CH]
                        src = bank(2 + (3 * m + c) % 4, 0, CH)
                        dve.wait_ge(dbank_full, df.up(1))
                        if first:
                            op = dve.tensor_copy(f, src)
                        else:
                            op = dve.tensor_tensor(f, f, src, ALU.add)
                        op.then_inc(dbank_free, 1)

            def turn(par, b2, first=False, last=False):
                add_down(0, first)
                ff_block(2 * (1 - par) + 1, b2)
                add_down(1, first)
                if not last:
                    ff_block(2 * par, b2 + 2)

            for j in range(3):
                ff_block(j, 2 * j)
            turn(0, 6, first=True)
            with repeat(dve, (NG - 3) // 2, tf, fd, cs, cw, ge, g3, gh, df, dfo) as i:
                turn(1, i * 8 + 10)
                turn(0, i * 8 + 14)
            turn(1, 2 * FB - 2, last=True)
            add_down(0, False)
            add_down(1, False)
            dfo.up(12 * 2)
            if dfo.due():
                dve.wait_ge(dbank_free, dfo.now())
            ys = Count(dve, orr, start=NC)
            for c in range(NC):
                cols = slice(c * CH, (c + 1) * CH)
                xin = Count(dve, x_in[c], start=32)
                rw.up(1), xin.up(16)
                dve.wait_ge(r_set, rw.now())
                dve.wait_ge(x_in[c], xin.now())
                for k in range(KB):
                    g = PV["fpost"] + k
                    op = dve.scalar_tensor_tensor(fx[:, KB + k, cols], fx[:, KB + k, cols], pars[:, g:g + 1],
                                                  rst[c][:, :], ALU.mult, ALU.mult)
                op.then_inc(orr, 1)
                dve.wait_ge(orr, ys.up(1))
                dve.tensor_tensor(fx[:, 0:KB, cols], fx[:, 0:KB, cols], fx[:, KB:2 * KB, cols], ALU.add)\
                    .then_inc(y_set, 1)


def kernel(**inputs):
    import numpy as np
    import concourse.bacc as bacc
    from concourse.bass_utils import run_bass_kernel_spmd

    g = {k: np.asarray(v)[0] for k, v in inputs.items()}
    xt = np.zeros((KB, P, T), np.float32)
    xt[:, :, 0:SEQ] = g["x_prompt"].T.reshape(KB, P, SEQ)
    xt[:, :, S0:T] = g["x_sample"].T.reshape(KB, P, DEC)
    xt = np.ascontiguousarray(xt.transpose(1, 0, 2))

    def tiles(w):
        r, c = w.shape
        return w.reshape(r // P, P, c // P, P).transpose(2, 1, 0, 3).reshape(c // P, P, r)

    w_in = g["w_in"]
    q, k, v, o = (tiles(w_in[:, j * D:(j + 1) * D]) for j in range(4))
    at = 4 * D
    gates = np.zeros((D, P), np.float32)
    gates[:, 0:NH] = w_in[:, at:at + NH]
    gates[:, 32:32 + NH] = w_in[:, at + NH:at + 2 * NH]
    at += 2 * NH
    ua, ub, ga, gb = (tiles(w_in[:, at + j * D:at + (j + 1) * D]) for j in range(4))
    pa, pb, wo = tiles(g["w_proj_a"]), tiles(g["w_proj_b"]), tiles(g["w_out"])
    up = tiles(g["w_up"])
    stream = [tiles(gates)[0]]
    for m in range(KB):
        stream += [ua[m], ub[m], q[m], k[m], v[m], o[m]]
    stream += list(ga)
    for m in range(KB):
        stream += [gb[m], pb[m]]
    stream += list(pa) + list(wo)
    wd = g["w_down"].reshape(NG, 2, P, 2, 4, P).transpose(0, 3, 2, 1, 4, 5).reshape(NG, 2, P, D)

    def ups(j):
        return [up[j], up[FB + j]]

    stream += ups(0) + ups(1) + ups(2)
    for n in range(1, NG):
        stream += [wd[n - 1, 0]] + ups(2 * n + 1) + [wd[n - 1, 1]]
        if n < NG - 1:
            stream += ups(2 * n + 2)
    stream += [wd[NG - 1, 0], wd[NG - 1, 1]]
    wts = np.stack(stream)
    assert len(stream) == N_TILES

    def cols(a):
        return a.reshape(-1, P).T

    par = np.zeros((P, NPAR), np.float32)
    for name, a in (("pre", g["norm_mix_pre"]), ("post", g["norm_mix_post"]), ("fpre", g["norm_ffn_pre"]),
                    ("fpost", g["norm_ffn_post"]), ("mnorm", g["mlstm_norm"]), ("convb", g["conv_b"]),
                    ("lng", g["conv_ln_g"]), ("lnb", g["conv_ln_b"]), ("bpb", g["b_proj_b"]),
                    ("bga", g["b_merge"][:D]), ("bgb", g["b_merge"][D:])):
        par[:, PV[name]:PV[name] + KB] = cols(a)
    par[:, PDW:PFF] = g["conv_dw"].reshape(CW, KB, P).transpose(2, 1, 0).reshape(P, KB * CW)

    def by_tile(a):
        return a.reshape(-1, 2, FB, P).transpose(3, 2, 1, 0)

    ffp = np.concatenate([by_tile(g["ffn_dw"]), by_tile(g["ffn_dw_b"][None])], axis=3)
    par[:, PFF:] = ffp.reshape(P, -1)
    gate_par = np.zeros((NH, 4), np.float32)
    gate_par[:, 0], gate_par[:, 1], gate_par[:, 2] = g["b_i"], g["b_f"], g["state_mlstm_m"][0]
    c_in = np.zeros((P, NH, 2, VW), np.float32)
    c_in[..., 0:DH] = g["state_mlstm_C"][0].reshape(NH, 2, P, DH).transpose(2, 0, 1, 3)
    c_in[..., DH] = g["state_mlstm_n"][0].reshape(NH, 2, P).transpose(2, 0, 1)
    conv_halo = g["cache_conv"][0].reshape(HALO, KB, P).transpose(2, 1, 0).reshape(P, KB * HALO)
    ffn_halo = by_tile(g["cache_ffn_conv"][0]).reshape(P, -1)

    nc = bacc.Bacc("TRN2", target_bir_lowering=False, num_devices=1)
    arrays, args = {}, []
    for name, a in (("x", xt), ("wts", wts), ("par", par), ("gate_par", gate_par), ("c_in", c_in),
                    ("conv_halo", conv_halo), ("ffn_halo", ffn_halo)):
        arrays[name] = np.ascontiguousarray(a)
        args.append(nc.dram_tensor(name, a.shape, F32, kind="ExternalInput").ap())
    for name, shape in (("y_out", (P, KB, T)), ("c_out", (2, P, NH, 2, VW)),
                        ("m_out", (NH, 2)), ("conv_tail", (2, P, KB, HALO)), ("ffn_tail", (P, 8 * FB))):
        args.append(nc.dram_tensor(name, shape, F32, kind="ExternalOutput").ap())
    build(nc, *args)
    r = run_bass_kernel_spmd(nc, [arrays], core_ids=[0]).results[0]

    y = r["y_out"].transpose(2, 1, 0).reshape(T, D)
    ft = r["ffn_tail"].reshape(P, FB, 2, 2, 2)
    out = [y[None, 0:SEQ], y[None, S0:T]]
    for n in range(2):
        state = r["c_out"][n].transpose(1, 2, 0, 3).reshape(1, 1, NH, DH, VW)
        out += [state[..., 0:DH], state[..., DH],
                r["m_out"][:, n].reshape(1, 1, NH),
                r["conv_tail"][n].transpose(2, 1, 0).reshape(1, 1, HALO, D),
                ft[:, :, :, n].transpose(3, 2, 1, 0).reshape(1, 1, 2, 2 * DFF)]
    return tuple(np.ascontiguousarray(a) for a in out)
```
